# Optimizing a Trainium2 kernel written in Bass

```python
import jax
import jax.numpy as jnp
from jax import lax
import numpy as np

D_MODEL = 1024
BATCH = 1
SEQ = 128
DEPTH = 2
DEC_BATCH = 1
DEC_SEQ = 256
PAST_LEN = 128

GRID_W = 64
N_HEADS_NA = 8
HEAD_DIM_NA = 64
WIN_H = 8
WIN_W = 16
N_HEADS_MLA = 8
QK_NOPE_DIM = 64
QK_ROPE_DIM = 32
V_HEAD_DIM = 64
Q_LORA_RANK = 256
KV_LORA_RANK = 128
D_NA = N_HEADS_NA * HEAD_DIM_NA
D_MLA = N_HEADS_MLA * V_HEAD_DIM
D_MIX = D_NA + D_MLA
PROJ_SPLITS = (D_NA, 2 * D_NA, 3 * D_NA, 3 * D_NA + Q_LORA_RANK, 3 * D_NA + Q_LORA_RANK + KV_LORA_RANK)
D_IN_PROJ = 3 * D_NA + Q_LORA_RANK + KV_LORA_RANK + QK_ROPE_DIM
N_EXPERTS = 16
N_EXPERT_GROUPS = 4
EXPERTS_PER_GROUP = N_EXPERTS // N_EXPERT_GROUPS
GROUP_SCORE_K = 2
TOP_K = 2
D_EXPERT = 512
ROPE_THETA = 10000.0
RMS_EPS = 1e-6
Q_BLOCK = 128
NA_SCALE = HEAD_DIM_NA ** -0.5
MLA_SCALE = (QK_NOPE_DIM + QK_ROPE_DIM) ** -0.5

kernel_name = 'natten_mla_grouped_moe_prefix_dit'

def _rms_norm(x, g):
    xf = x.astype(jnp.float32)
    y = xf * lax.rsqrt(jnp.mean(xf * xf, axis=-1, keepdims=True) + RMS_EPS)
    return (y * g.astype(jnp.float32)).astype(x.dtype)

def _modulation(cond, w_ada, b_ada):
    return jnp.split(jax.nn.silu(cond) @ w_ada + b_ada, 6, axis=-1)

def _modulate(x, g, shift, scale):
    return _rms_norm(x, g) * (1 + scale) + shift

def _axial_rope(x, rows, cols):
    half = QK_ROPE_DIM // 2
    freqs = 1.0 / (ROPE_THETA ** (jnp.arange(0, half, 2, dtype=jnp.float32) / half))

    def rot(xa, pos):
        ang = pos.astype(jnp.float32)[:, None] * freqs
        cos = jnp.cos(ang)[None, :, None, :]
        sin = jnp.sin(ang)[None, :, None, :]
        x1, x2 = jnp.split(xa.astype(jnp.float32), 2, axis=-1)
        return jnp.concatenate([x1 * cos - x2 * sin, x2 * cos + x1 * sin], axis=-1).astype(xa.dtype)

    return jnp.concatenate([rot(x[..., :half], rows), rot(x[..., half:], cols)], axis=-1)

def _block_attention(q, k, v, scale):
    b, lq, h, dk = q.shape
    qb = jnp.moveaxis(q.reshape(b, lq // Q_BLOCK, Q_BLOCK, h, dk), 1, 0)

    def one(qblk):
        s = jnp.einsum('bqhd,bkhd->bhqk', qblk, k).astype(jnp.float32) * scale
        p = jax.nn.softmax(s, axis=-1).astype(v.dtype)
        return jnp.einsum('bhqk,bkhd->bqhd', p, v)

    o = lax.map(one, qb)
    return jnp.moveaxis(o, 0, 1).reshape(b, lq, h, v.shape[-1])

def _neighbourhood_attention(q, k, v, k_ctx, v_ctx, rpb):
    b, s, h, d = q.shape
    rows = s // GRID_W
    kh = min(WIN_H, rows)
    ncb = GRID_W // WIN_W
    band = 2 * WIN_W
    qg = q.reshape(b, rows, ncb, WIN_W, h, d)
    kg = k.reshape(b, rows, GRID_W, h, d)
    vg = v.reshape(b, rows, GRID_W, h, d)
    col_start = jnp.clip(jnp.arange(ncb) * WIN_W - WIN_W // 2, 0, GRID_W - band)
    col_idx = col_start[:, None] + jnp.arange(band)
    q_col = jnp.arange(GRID_W).reshape(ncb, WIN_W)
    win_start = jnp.clip(q_col - WIN_W // 2, 0, GRID_W - WIN_W)
    key_col = col_idx[:, None, :]
    col_mask = (key_col >= win_start[..., None]) & (key_col < win_start[..., None] + WIN_W)
    col_off = jnp.clip(key_col - q_col[..., None] + WIN_W - 1, 0, 2 * WIN_W - 2)
    n_win = kh * band

    def one_row(r):
        rs = jnp.clip(r - kh // 2, 0, rows - kh)
        k_band = lax.dynamic_slice_in_dim(kg, rs, kh, axis=1)[:, :, col_idx]
        v_band = lax.dynamic_slice_in_dim(vg, rs, kh, axis=1)[:, :, col_idx]
        qr = lax.dynamic_index_in_dim(qg, r, axis=1, keepdims=False)
        row_off = rs + jnp.arange(kh) - r + WIN_H - 1
        bias = rpb[:, row_off[None, None, :, None], col_off[:, :, None, :]]
        s_win = jnp.einsum('bnqhd,bknwhd->bhnqkw', qr, k_band).astype(jnp.float32) * NA_SCALE + bias.astype(jnp.float32)
        s_win = jnp.where(col_mask[:, :, None, :], s_win, -jnp.inf)
        s_ctx = jnp.einsum('bnqhd,bchd->bhnqc', qr, k_ctx).astype(jnp.float32) * NA_SCALE
        p = jax.nn.softmax(jnp.concatenate([s_win.reshape(b, h, ncb, WIN_W, n_win), s_ctx], axis=-1), axis=-1).astype(v.dtype)
        p_win = p[..., :n_win].reshape(b, h, ncb, WIN_W, kh, band)
        return (jnp.einsum('bhnqkw,bknwhd->bnqhd', p_win, v_band)
                + jnp.einsum('bhnqc,bchd->bnqhd', p[..., n_win:], v_ctx))

    o = lax.map(one_row, jnp.arange(rows))
    return jnp.moveaxis(o, 0, 1).reshape(b, s, h, d)

def _project(h, w_in, q_norm_g, w_uq, kv_norm_g):
    b, l, _ = h.shape
    q_na, k_na, v_na, cq, ckv, k_rope = jnp.split(h @ w_in, PROJ_SPLITS, axis=-1)
    heads = lambda t: t.reshape(b, l, N_HEADS_NA, HEAD_DIM_NA)
    q_mla = (_rms_norm(cq, q_norm_g) @ w_uq).reshape(b, l, N_HEADS_MLA, QK_NOPE_DIM + QK_ROPE_DIM)
    return heads(q_na), heads(k_na), heads(v_na), q_mla, _rms_norm(ckv, kv_norm_g), k_rope

def _mla_kv(ckv, k_rope, w_ukv):
    b, l, _ = ckv.shape
    kv = (ckv @ w_ukv).reshape(b, l, N_HEADS_MLA, QK_NOPE_DIM + V_HEAD_DIM)
    k_r = jnp.broadcast_to(k_rope[:, :, None, :], (b, l, N_HEADS_MLA, QK_ROPE_DIM))
    return jnp.concatenate([kv[..., :QK_NOPE_DIM], k_r], axis=-1), kv[..., QK_NOPE_DIM:]

def _grouped_moe(h, w_router, b_router, w_gate, w_up, w_down):
    shape = h.shape
    t = h.reshape(-1, shape[-1])
    n = t.shape[0]
    aff = jax.nn.sigmoid((t @ w_router).astype(jnp.float32))
    sel = (aff + b_router.astype(jnp.float32)).reshape(n, N_EXPERT_GROUPS, EXPERTS_PER_GROUP)
    group_score = lax.top_k(sel, GROUP_SCORE_K)[0].sum(-1)
    g_idx = jnp.argmax(group_score, axis=-1)
    in_group = jnp.take_along_axis(sel, g_idx[:, None, None], axis=1)[:, 0]
    _, local = lax.top_k(in_group, TOP_K)
    e_idx = g_idx[:, None] * EXPERTS_PER_GROUP + local
    w_sel = jnp.take_along_axis(aff, e_idx, axis=1)
    w_sel = w_sel / jnp.sum(w_sel, axis=-1, keepdims=True)
    gates = jnp.sum(jax.nn.one_hot(e_idx, N_EXPERTS, dtype=jnp.float32) * w_sel[..., None], axis=1)
    hid = jax.nn.silu(jnp.einsum('nd,edf->nef', t, w_gate)) * jnp.einsum('nd,edf->nef', t, w_up)
    out = jnp.einsum('nef,efd->nd', hid * gates[..., None].astype(hid.dtype), w_down)
    return out.reshape(shape)

def _context_layer(x, mod, lw):
    n1, n2, w_in, qn, w_uq, kvn, w_ukv, w_out, w_router, b_router, w_gate, w_up, w_down = lw
    sh1, sc1, g1, sh2, sc2, g2 = mod
    b, l, _ = x.shape
    q_na, k_na, v_na, q_mla, ckv, k_rope = _project(_modulate(x, n1, sh1, sc1), w_in, qn, w_uq, kvn)
    o_na = _block_attention(q_na, k_na, v_na, NA_SCALE)
    k_mla, v_mla = _mla_kv(ckv, k_rope, w_ukv)
    o_mla = _block_attention(q_mla, k_mla, v_mla, MLA_SCALE)
    o = jnp.concatenate([o_na.reshape(b, l, D_NA), o_mla.reshape(b, l, D_MLA)], axis=-1) @ w_out
    x = x + g1 * o
    x = x + g2 * _grouped_moe(_modulate(x, n2, sh2, sc2), w_router, b_router, w_gate, w_up, w_down)
    return x, (k_na, v_na, ckv, k_rope)

def _latent_layer(x, mod, lw, rpb, ctx, rows_pos, cols_pos):
    n1, n2, w_in, qn, w_uq, kvn, w_ukv, w_out, w_router, b_router, w_gate, w_up, w_down = lw
    sh1, sc1, g1, sh2, sc2, g2 = mod
    k_ctx_na, v_ctx_na, ckv_ctx, krope_ctx = ctx
    b, s, _ = x.shape
    q_na, k_na, v_na, q_mla, ckv, k_rope = _project(_modulate(x, n1, sh1, sc1), w_in, qn, w_uq, kvn)
    o_na = _neighbourhood_attention(q_na, k_na, v_na, k_ctx_na, v_ctx_na, rpb)
    q_mla = jnp.concatenate([q_mla[..., :QK_NOPE_DIM],
                             _axial_rope(q_mla[..., QK_NOPE_DIM:], rows_pos, cols_pos)], axis=-1)
    k_rope = _axial_rope(k_rope[:, :, None, :], rows_pos, cols_pos)[:, :, 0, :]
    k_lat, v_lat = _mla_kv(ckv, k_rope, w_ukv)
    k_c, v_c = _mla_kv(ckv_ctx, krope_ctx, w_ukv)
    o_mla = _block_attention(q_mla, jnp.concatenate([k_c, k_lat], axis=1),
                             jnp.concatenate([v_c, v_lat], axis=1), MLA_SCALE)
    o = jnp.concatenate([o_na.reshape(b, s, D_NA), o_mla.reshape(b, s, D_MLA)], axis=-1) @ w_out
    x = x + g1 * o
    x = x + g2 * _grouped_moe(_modulate(x, n2, sh2, sc2), w_router, b_router, w_gate, w_up, w_down)
    return x

def setup_inputs(seed: int = 0) -> dict:
    key = jax.random.key(seed)
    ks = jax.random.split(key, 25)
    nrm = lambda k, shape, scale: jax.random.normal(k, shape, jnp.float32) * scale
    gain = lambda k, shape: 1.0 + 0.05 * jax.random.normal(k, shape, jnp.float32)
    return {
        'x_prompt': nrm(ks[0], (BATCH, SEQ, D_MODEL), 1.0),
        'x_sample': nrm(ks[1], (DEC_BATCH, DEC_SEQ, D_MODEL), 1.0),
        'cache_nat_k': nrm(ks[2], (DEC_BATCH, DEPTH, PAST_LEN, N_HEADS_NA, HEAD_DIM_NA), 1.0),
        'cache_nat_v': nrm(ks[3], (DEC_BATCH, DEPTH, PAST_LEN, N_HEADS_NA, HEAD_DIM_NA), 1.0),
        'cache_mla_ckv': nrm(ks[4], (DEC_BATCH, DEPTH, PAST_LEN, KV_LORA_RANK), 1.0),
        'cache_mla_krope': nrm(ks[5], (DEC_BATCH, DEPTH, PAST_LEN, QK_ROPE_DIM), 1.0),
        'c': nrm(ks[6], (DEC_BATCH, D_MODEL), 1.0),
        'c_ctx': nrm(ks[7], (D_MODEL,), 1.0),
        'norm1_g': gain(ks[8], (DEPTH, D_MODEL)),
        'norm2_g': gain(ks[9], (DEPTH, D_MODEL)),
        'w_ada': nrm(ks[10], (DEPTH, D_MODEL, 6 * D_MODEL), 0.2 * D_MODEL ** -0.5),
        'b_ada': nrm(ks[11], (DEPTH, 6 * D_MODEL), 0.01),
        'w_in': nrm(ks[12], (DEPTH, D_MODEL, D_IN_PROJ), D_MODEL ** -0.5),
        'q_norm_g': gain(ks[13], (DEPTH, Q_LORA_RANK)),
        'w_uq': nrm(ks[14], (DEPTH, Q_LORA_RANK, N_HEADS_MLA * (QK_NOPE_DIM + QK_ROPE_DIM)), Q_LORA_RANK ** -0.5),
        'kv_norm_g': gain(ks[15], (DEPTH, KV_LORA_RANK)),
        'w_ukv': nrm(ks[16], (DEPTH, KV_LORA_RANK, N_HEADS_MLA * (QK_NOPE_DIM + V_HEAD_DIM)), KV_LORA_RANK ** -0.5),
        'rpb': nrm(ks[17], (DEPTH, N_HEADS_NA, 2 * WIN_H - 1, 2 * WIN_W - 1), 0.02),
        'w_out': nrm(ks[18], (DEPTH, D_MIX, D_MODEL), D_MIX ** -0.5),
        'w_router': nrm(ks[19], (D_MODEL, N_EXPERTS), D_MODEL ** -0.5),
        'b_router': nrm(ks[20], (N_EXPERTS,), 0.01),
        'w_gate': nrm(ks[21], (DEPTH, N_EXPERTS, D_MODEL, D_EXPERT), D_MODEL ** -0.5),
        'w_up': nrm(ks[22], (DEPTH, N_EXPERTS, D_MODEL, D_EXPERT), D_MODEL ** -0.5),
        'w_down': nrm(ks[23], (DEPTH, N_EXPERTS, D_EXPERT, D_MODEL), D_EXPERT ** -0.5),
        'final_norm_g': gain(ks[24], (D_MODEL,)),
    }

def reference(x_prompt, x_sample, cache_nat_k, cache_nat_v, cache_mla_ckv, cache_mla_krope, c, c_ctx,
              norm1_g, norm2_g, w_ada, b_ada, w_in, q_norm_g, w_uq, kv_norm_g, w_ukv, rpb, w_out,
              w_router, b_router, w_gate, w_up, w_down, final_norm_g):
    s = x_sample.shape[1]
    t = jnp.arange(s)
    rows_pos = t // GRID_W
    cols_pos = t % GRID_W
    xc = x_prompt
    xs = x_sample
    nat_k, nat_v, mla_ckv, mla_krope = [], [], [], []
    for l in range(DEPTH):
        lw = (norm1_g[l], norm2_g[l], w_in[l], q_norm_g[l], w_uq[l], kv_norm_g[l], w_ukv[l], w_out[l],
              w_router, b_router, w_gate[l], w_up[l], w_down[l])
        mod_ctx = _modulation(c_ctx, w_ada[l], b_ada[l])
        mod_lat = [m[:, None, :] for m in _modulation(c, w_ada[l], b_ada[l])]
        xc, (k_na, v_na, ckv, k_rope) = _context_layer(xc, mod_ctx, lw)
        nat_k.append(k_na)
        nat_v.append(v_na)
        mla_ckv.append(ckv)
        mla_krope.append(k_rope)
        ctx = (cache_nat_k[:, l], cache_nat_v[:, l], cache_mla_ckv[:, l], cache_mla_krope[:, l])
        xs = _latent_layer(xs, mod_lat, lw, rpb[l], ctx, rows_pos, cols_pos)
    y_prompt = _rms_norm(xc, final_norm_g)
    y_sample = _rms_norm(xs, final_norm_g)
    new_nat_k = jnp.stack(nat_k, axis=1)
    new_nat_v = jnp.stack(nat_v, axis=1)
    new_mla_ckv = jnp.stack(mla_ckv, axis=1)
    new_mla_krope = jnp.stack(mla_krope, axis=1)
    return (y_prompt, y_sample, new_nat_k, new_nat_v, new_mla_ckv, new_mla_krope)


_drawn_inputs = setup_inputs


def setup_inputs(seed=0):
    import zlib

    import numpy as np

    out = dict(_drawn_inputs(seed))
    spreads = {}
    factors = {'cache_nat_k': 4.157,
     'cache_nat_v': 3.503,
     'cache_mla_ckv': 6.019,
     'cache_mla_krope': 8.0,
     'norm2_g': 2.846,
     'b_ada': 3.522,
     'q_norm_g': 8.0,
     'w_uq': 2.919,
     'rpb': 171.599,
     'b_router': 2.803}
    for name, (base, spread) in spreads.items():
        noise = np.random.default_rng([zlib.crc32(name.encode()), seed]).standard_normal(out[name].shape)
        drawn = base * np.exp(spread * noise) if base else spread * noise
        out[name] = jnp.asarray(drawn.astype(out[name].dtype))
    for name, factor in factors.items():
        out[name] = (out[name] * factor).astype(out[name].dtype)
    return out
```

```python
import numpy as np
import concourse.bass as bass
from concourse import mybir
from contextlib import ExitStack

P = 128
D = 1024
KD = D // P
CTX, LAT = 128, 256
TOK = CTX + LAT
NT = TOK // P
DEPTH = 2
HEADS, HD = 8, 64
ROPE = 32
QKD = HD + ROPE
RANK_Q, RANK_KV = 256, 128
D_NA = HEADS * HD
REST = RANK_Q + RANK_KV + ROPE
PAST = 128
GRID = 64
WIN_H, WIN_W = 8, 16
RPB_ROWS, RPB_COLS = 2 * WIN_H - 1, 2 * WIN_W - 1
E_ALL, GROUPS, E_GROUP = 16, 4, 4
F = 512
SLOT = 4096
NSLOT = 4
EPS = 1e-6
NA_SCALE = HD ** -0.5
MLA_SCALE = QKD ** -0.5
SEGS = ((0, CTX, 0), (CTX, TOK, 1))

ADA_EARLY = 4
W_REST, W_V, W_Q, W_K, W_UQ, W_UKV = 4, 5, 6, 7, 8, 9
ADA_LATE = 10
W_OUT = 18
W_MOE = 20
MAIN_SLOTS = W_MOE + GROUPS * 3 * E_GROUP
PASSES = GROUPS + 2
LAYER_SLOTS = W_MOE + PASSES * 3 * E_GROUP
assert W_MOE % NSLOT == 0 and (3 * E_GROUP) % NSLOT == 0

IT_REST, IT_V, IT_QK, IT_KOUT, IT_KC, IT_CQT, IT_CKVT, IT_KRT = 0, 3, 6, 14, 15, 16, 18, 19
IT_QM, IT_VM, IT_KM, IT_QMT, IT_OT, IT_HTOK, ITEMS = 20, 26, 30, 38, 46, 54, 60
UNITS = 24
STEPS = 512
MSTEPS = 32
SKEW = 512
SKEW_HEAD = P * (SKEW + 1)
OUT_DMAS = 4

C_ID, C_TRI, C_ONE, C_IOTA, C_MASK, C_COS, C_SIN, C_GIDX, C_N = 0, 128, 256, 384, 512, 576, 640, 704, 712


class Steps:

    def __init__(self, eng, sem, base):
        self.eng, self.sem, self.base, self.n = eng, sem, base, 0

    def did(self, ins):
        ins.then_inc(self.sem, 1)
        self.n += 1

    def sync(self):
        self.eng.wait_ge(self.sem, self.base + self.n)

    def close(self, share):
        assert self.n <= share, self.n
        if self.n < share:
            self.eng.sem_inc(self.sem, share - self.n)


def build(nc, a, outs, scratch, skewed):
    f32, i32 = mybir.dt.float32, mybir.dt.int32
    ALU, ACT, AX = mybir.AluOpType, mybir.ActivationFunctionType, mybir.AxisListType

    with ExitStack() as ctx:
        arena = ctx.enter_context(nc.sbuf_tensor("arena", [P, 53000], f32))
        top = [0]

        def take(n):
            at = top[0]
            top[0] += n
            assert top[0] <= 53000, top[0]
            return arena[:, at:at + n]

        def tiles(ap, n):
            return ap.rearrange("p (a b) -> p a b", a=n)

        ring = take(NSLOT * SLOT)
        xT = tiles(take(KD * TOK), KD)
        hT_flat = take(KD * TOK)
        hT = tiles(hT_flat, KD)
        wide = take(KD * TOK)
        xn = tiles(wide, KD)
        tokx = tiles(wide, NT)
        qtok = tiles(wide[:, 0:NT * HEADS * QKD], NT)
        otok = tiles(wide, NT)
        qkT_flat = take(8 * TOK)
        qkT = tiles(qkT_flat, 8)
        kcT = tiles(take(4 * P), 4)
        kc_tok = take(D_NA)
        vc = take(D_NA)
        vtok = tiles(take(NT * D_NA), NT)
        probs_flat = take(8 * TOK)
        prob = probs_flat[:, 0:4 * TOK].rearrange("p (u i n) -> p u i n", u=2, i=2)
        probT = probs_flat[:, 4 * TOK:8 * TOK].rearrange("p (u i n) -> p u i n", u=2, i=2)
        rest = tiles(probs_flat[:, 0:NT * REST], NT)
        cqn = tiles(probs_flat[:, 1248:1248 + NT * RANK_Q], NT)
        cqT = tiles(probs_flat[:, 2016:2016 + 2 * TOK], 2)
        ckvT = take(4 * P)
        krT = take(4 * P)
        ckvn = tiles(take(4 * P), 4)
        kr = tiles(take(4 * QKD), 4)
        latent_flat = take(HEADS * TOK + HEADS * 4 * P + 4 * D_NA)
        qmT = tiles(latent_flat[:, 0:HEADS * TOK], HEADS)
        kmT = tiles(latent_flat[:, 3072:3072 + HEADS * 4 * P], HEADS)
        vm = tiles(latent_flat[:, 7168:7168 + 4 * D_NA], 4)
        bias_flat = take(HEADS * 6 * GRID)
        bias = tiles(bias_flat, HEADS)
        k_out = take(D_NA)
        htok = tiles(latent_flat[:, 0:3072], NT)
        hg = tiles(latent_flat[:, 3072:4096], KD)
        y_sb = latent_flat[:, 4096:5120]
        sel_m = tiles(latent_flat[:, 5120:5504], NT)
        selT = latent_flat[:, 5504:5892]
        th = latent_flat[:, 5892:6404]
        t1 = latent_flat[:, 6404:6916]
        hid = [latent_flat[:, 6916 + 512 * i:7428 + 512 * i] for i in range(2)]
        hidT = [tiles(latent_flat[:, 7940 + 512 * i:8452 + 512 * i], 4) for i in range(2)]
        consts = take(C_N)
        ident = consts[:, C_ID:C_ID + P]
        tri = consts[:, C_TRI:C_TRI + P]
        ones = consts[:, C_ONE:C_ONE + P]
        iota = consts[:, C_IOTA:C_IOTA + P]
        mask = consts[:, C_MASK:C_MASK + GRID]
        cos = tiles(consts[:, C_COS:C_COS + 64], 2)
        sin = tiles(consts[:, C_SIN:C_SIN + 64], 2)
        gidx = tiles(consts[:, C_GIDX:C_GIDX + 8], 2)
        w_r = tiles(take(KD * E_ALL), KD)
        b_r = take(E_ALL)
        rows = k_out[:, 0:3 * P]
        vec = tiles(take(3 * 66), 3)
        cond = take(16).rearrange("p (k s) -> p k s", k=8)
        cond_e = take(16)
        kvg = tiles(take(2 * P), 2)
        rstd = take(TOK)
        mod = take(96).rearrange("p (c k s) -> p c k s", c=6, k=KD)
        gain = take(32).rearrange("p (n k s) -> p n k s", n=2, k=KD)
        eps = take(1)
        stat = take(6)
        rstat = take(6)
        neg_max = take(8)
        sums = take(8)
        rsum = take(4)
        rope_t = take(256)
        pad = bias_flat[:, 0:RPB_ROWS * GRID]
        rt = tiles(take(12 * 48), 12)
        cmp = take(4 * 48)
        one_hot, rk1, slot_of = tiles(take(12), NT), tiles(take(12), NT), tiles(take(18), NT)
        gates4 = tiles(take(12), NT)
        small = tiles(take(8 * 8), 8)
        prod = tiles(take(12), NT)
        ctl_f = take(4)
        ctl = ctx.enter_context(nc.sbuf_tensor("ctl", [P, 4], i32))

        psum = ctx.enter_context(nc.psum_tensor("psum", [P, 8, 512], f32))
        bank = [psum[:, b, :] for b in range(8)]

        def sem(name):
            return ctx.enter_context(nc.semaphore(name))

        consts_in, rows_in, x_in, router_in, pad_in = (sem(n) for n in ("consts_in", "rows_in", "x_in", "router_in", "pad_in"))
        cache_in = sem("cache_in")
        pad_zero, skew_stored, pad_ready, rpb_stored, bias_in, bias_ready, kr_zero = (sem(n) for n in (
            "pad_zero", "skew_stored", "pad_ready", "rpb_stored", "bias_in", "bias_ready", "kr_zero"))
        x_ps, x_evac = sem("x_ps"), sem("x_evac")
        vec_ps, vec_ready, cond_ready, eps_ready = sem("vec_ps"), sem("vec_ready"), sem("cond_ready"), sem("eps_ready")
        cond_exp = sem("cond_exp")
        slot_full = [sem(f"slot_full{i}") for i in range(NSLOT)]
        slot_free = sem("slot_free")
        mod_ready = sem("mod_ready")
        sq_ready, ss_ps, std_ready, xn_ready, h_ready = (sem(n) for n in ("sq_ready", "ss_ps", "std_ready", "xn_ready", "h_ready"))
        item_ps, item_act, item_dve = sem("item_ps"), sem("item_act"), sem("item_dve")
        lora_stat, lora_norm, kr_ready, q_roped, kr_spread = (sem(n) for n in ("lora_stat", "lora_norm", "kr_ready", "q_roped", "kr_spread"))
        score_ps, max_ready, exp_ready, probT_ps, probT_act, probT_dve, o_ps, o_ready = (sem(n) for n in (
            "score_ps", "max_ready", "exp_ready", "probT_ps", "probT_act", "probT_dve", "o_ps", "o_ready"))
        wo_ps, x_updated = sem("wo_ps"), sem("x_updated")
        logit_ps, logit_exp, hot_ready, rank_ps, routed = (sem(n) for n in ("logit_ps", "logit_exp", "hot_ready", "rank_ps", "routed"))
        sel_ready, gather_ps, hg_act, hg_dve, selT_ps, selT_ready = (sem(n) for n in (
            "sel_ready", "gather_ps", "hg_act", "hg_dve", "selT_ps", "selT_ready"))
        tanh_ready, hid_ready, hidT_ps, hidT_ready, y_act, y_dve, scat_ps, scat_done = (sem(n) for n in (
            "tanh_ready", "hid_ready", "hidT_ps", "hidT_ready", "y_act", "y_dve", "scat_ps", "scat_done"))
        act_step, dve_step, dve_mstep, pool_step = sem("act_step"), sem("dve_step"), sem("dve_mstep"), sem("pool_step")
        past = sem("past")
        out_free, stored_y = sem("out_free"), sem("stored_y")
        stored, y_ready, y_ps = sem("stored"), sem("y_ready"), sem("y_ps")
        block = ctx.enter_context(nc.Block())

        def item_free(eng, l, j):
            prev = j - 4
            s = item_act if j % 2 == 0 else item_dve
            if prev >= 0:
                eng.wait_ge(s, ITEMS // 2 * l + prev // 2 + 1)

        def item_wait(eng, l, j):
            eng.wait_ge(item_act if j % 2 == 0 else item_dve, ITEMS // 2 * l + j // 2 + 1)

        def passed(eng):
            eng.sem_inc(past, 1)

        def used(l, n):
            return LAYER_SLOTS * l + (NSLOT + n)

        def pass_used(l, p):
            return LAYER_SLOTS * l + 12 * p + (NSLOT + W_MOE)

        def slot(n):
            s = n % NSLOT
            return ring[:, s * SLOT:(s + 1) * SLOT]

        def overflow(eng, l, o, owned, body):
            used = eng.value_load(ctl[0:1, o:o + 1], min_val=0, max_val=1)
            with eng.If(used > 0):
                body()
            with eng.Else():
                for s, before, share in owned:
                    eng.wait_ge(s, before)
                    eng.sem_inc(s, share)

        @block.sync
        def _(sp):
            sp.dma_start(consts, a["consts"]).then_inc(consts_in, 16)
            sp.dma_start(tokx[:, 0, :], a["x_prompt"][0, :, :]).then_inc(x_in, 16)
            sp.dma_start(tokx[:, 1:3, :], a["x_sample"].rearrange("b (t p) d -> p (b t) d", p=P)).then_inc(x_in, 16)
            for i in range(NSLOT):
                sp.sem_inc(slot_free, 1)

            def load(l, n, dst, src, count=None):
                sp.wait_ge(slot_free, LAYER_SLOTS * l + (n if count is None else count) + 1)
                passed(sp)
                sp.dma_start(dst, src).then_inc(slot_full[n % NSLOT], 16)

            def cols(w, l, lo, hi):
                return w[bass.ds(l, 1), :, lo:hi].rearrange("a (k p) n -> p (a k) n", p=P)

            def expert_loads(l, group, first):
                seq = [("g", 0), ("u", 0), ("g", 1), ("u", 1), ("d", 0), ("g", 2), ("u", 2), ("d", 1),
                       ("g", 3), ("u", 3), ("d", 2), ("d", 3)]
                for i, (kind, e) in enumerate(seq):
                    w = {"g": a["w_gate"], "u": a["w_up"], "d": a["w_down"]}[kind]
                    src = w[bass.ds(l, 1), bass.ds(group * E_GROUP + e, 1), :, :].rearrange("a b (k p) n -> p (a b k) n", p=P)
                    load(l, i, slot(i).rearrange("p (k n) -> p k n", k=4 if kind == "d" else 8), src, first + i)

            with sp.Fori(0, DEPTH) as l:
                for n in range(ADA_EARLY):
                    load(l, n, tiles(slot(n), KD), cols(a["w_ada"], l, 512 * n, 512 * n + 512))
                load(l, W_REST, tiles(slot(W_REST)[:, 0:KD * REST], KD), cols(a["w_in"], l, 3 * D_NA, 3 * D_NA + REST))
                load(l, W_V, tiles(slot(W_V), KD), cols(a["w_in"], l, 2 * D_NA, 3 * D_NA))
                load(l, W_Q, tiles(slot(W_Q), KD), cols(a["w_in"], l, 0, D_NA))
                load(l, W_K, tiles(slot(W_K), KD), cols(a["w_in"], l, D_NA, 2 * D_NA))
                load(l, W_UQ, tiles(slot(W_UQ)[:, 0:2 * HEADS * QKD], 2), cols(a["w_uq"], l, 0, HEADS * QKD))
                load(l, W_UKV, tiles(slot(W_UKV)[:, 0:D], 1), cols(a["w_ukv"], l, 0, D))
                for i in range(8):
                    c = 512 * (ADA_EARLY + i)
                    load(l, ADA_LATE + i, tiles(slot(ADA_LATE + i), KD), cols(a["w_ada"], l, c, c + 512))
                for i in range(2):
                    load(l, W_OUT + i, tiles(slot(W_OUT + i), KD), cols(a["w_out"], l, 512 * i, 512 * i + 512))
                with sp.Fori(0, GROUPS) as p:
                    expert_loads(l, p, 12 * p + W_MOE)
                sp.wait_ge(routed, l + 1)
                passed(sp)
                for o in range(2):
                    p = GROUPS + o
                    group = sp.value_load(ctl[0:1, 2 + o:3 + o], min_val=0, max_val=GROUPS - 1)
                    owned = [(slot_full[s], 16 * (LAYER_SLOTS // NSLOT * l + (W_MOE + 12 * p) // NSLOT), 48) for s in range(NSLOT)]
                    overflow(sp, l, o, owned, lambda: expert_loads(l, group, W_MOE + 12 * p))
            for t in range(NT):
                sp.wait_ge(y_ready, t + 1)
                dst = outs[0][0, :, :] if t == 0 else outs[1][0, P * (t - 1):P * t, :]
                sp.dma_start(dst, tokx[:, t, :]).then_inc(stored_y, 16)
            sp.wait_ge(out_free, DEPTH + 1)
            sp.wait_ge(stored_y, 16 * NT)

        @block.gpsimd
        def _(pool):
            st = Steps(pool, pool_step, 0)
            pool.memset(pad[0:16, :], 0.0).then_inc(pad_zero, 1)
            pool.memset(kr[:, :, :], 0.0).then_inc(kr_zero, 1)
            pool.memset(rows[:, :], 0.0).then_inc(kr_zero, 1)
            pool.wait_ge(pad_zero, 1)
            padv = pad[0:16, :].rearrange("p (r c) -> p r c", r=RPB_ROWS)
            pool.dma_start(padv[:, :, 0:RPB_COLS], a["rpb"].rearrange("l h r c -> (l h) r c")).then_inc(pad_in, 16)
            pool.wait_ge(kr_zero, 2)
            for l in range(DEPTH):
                at = rows[:, P * l:P * l + P]
                pool.dma_start(at[0:48, :], a["b_ada"][l, :].rearrange("(r c) -> r c", c=P)).then_inc(rows_in, 16)
                pool.dma_start(at[48:56, :], a["norm1_g"][l, :].rearrange("(r c) -> r c", c=P)).then_inc(rows_in, 16)
                pool.dma_start(at[56:64, :], a["norm2_g"][l, :].rearrange("(r c) -> r c", c=P)).then_inc(rows_in, 16)
                pool.dma_start(at[64:66, :], a["q_norm_g"][l, :].rearrange("(r c) -> r c", c=P)).then_inc(rows_in, 16)
            at = rows[:, 2 * P:3 * P]
            pool.dma_start(at[0:8, :], a["c_ctx"].rearrange("(r c) -> r c", c=P)).then_inc(rows_in, 16)
            pool.dma_start(at[8:16, :], a["c"][0, :].rearrange("(r c) -> r c", c=P)).then_inc(rows_in, 16)
            pool.dma_start(at[16:24, :], a["final_norm_g"].rearrange("(r c) -> r c", c=P)).then_inc(rows_in, 16)
            pool.dma_start(w_r, a["w_router"].rearrange("(k p) e -> p k e", p=P)).then_inc(router_in, 16)
            pool.dma_start(b_r, a["b_router"].partition_broadcast(P)).then_inc(router_in, 16)
            for l in range(DEPTH):
                pool.dma_start(kvg[:, l, :], a["kv_norm_g"][l, :].partition_broadcast(P)).then_inc(router_in, 16)
            pool.wait_ge(pad_in, 16)
            pool.tensor_scalar(pad[0:16, :], pad[0:16, :], 1.0 / NA_SCALE, None, ALU.mult).then_inc(pad_ready, 1)
            pool.wait_ge(pad_ready, 1)
            pool.dma_start(scratch.ap(), pad[0:16, :]).then_inc(rpb_stored, 16)
            pool.wait_ge(rpb_stored, 16)
            pitch = RPB_ROWS * GRID
            for l in range(DEPTH):
                src = bass.AP(scratch, l * HEADS * pitch + 5 * GRID + WIN_W - P, [[0, P], [pitch, HEADS], [1, SKEW]])
                dst = bass.AP(skewed, l * HEADS * SKEW_HEAD, [[SKEW + 1, P], [SKEW_HEAD, HEADS], [1, SKEW]])
                pool.dma_start(dst, src).then_inc(skew_stored, 16)
            pool.wait_ge(skew_stored, 32)
            pool.wait_ge(consts_in, 16)
            pool.sem_inc(out_free, 1)
            pool.sem_inc(o_ready, 1)

            def skew_rows(l):
                v = skewed.ap()[bass.ds(l, 1), :, 0:P * SKEW].rearrange("l h (p n) -> p (l h) n", p=P)
                return v[:, :, P - 1:P - 1 + 6 * GRID]

            with pool.Fori(0, DEPTH) as l:
                st = Steps(pool, pool_step, 8 * l)
                pool.wait_ge(o_ready, UNITS * l + 1)
                pool.dma_start(kc_tok, a["cache_nat_k"][0, bass.ds(l, 1), :, :, :].rearrange("l p h d -> p (l h d)")).then_inc(cache_in, 16)
                pool.dma_start(vc, a["cache_nat_v"][0, bass.ds(l, 1), :, :, :].rearrange("l p h d -> p (l h d)")).then_inc(cache_in, 16)
                pool.dma_start(ckvn[:, 1, :], a["cache_mla_ckv"][0, bass.ds(l, 1), :, :].rearrange("l p d -> p (l d)")).then_inc(cache_in, 16)
                pool.dma_start(kr[:, 1, HD:QKD], a["cache_mla_krope"][0, bass.ds(l, 1), :, :].rearrange("l p d -> p (l d)")).then_inc(cache_in, 16)
                pool.dma_start(bias, skew_rows(l)).then_inc(bias_in, 16)
                pool.wait_ge(bias_in, 16 * l + 16)
                b4 = bias.rearrange("p h (j c) -> p (h j) c", c=GRID)
                pool.tensor_tensor(b4, b4, mask.unsqueeze(1).to_broadcast([P, HEADS * 6, GRID]), ALU.add).then_inc(bias_ready, 1)
                pool.wait_ge(bias_ready, l + 1)
                item_wait(pool, l, IT_KRT)
                passed(pool)
                pool.tensor_copy(kmT[HD:QKD, :, :], krT[HD:QKD, :].unsqueeze(1).to_broadcast([ROPE, HEADS, 4 * P])).then_inc(kr_spread, 1)
                item_wait(pool, l, IT_KOUT)
                passed(pool)
                pool.dma_start(outs[2][0, bass.ds(l, 1), :, :, :].rearrange("l p h d -> p (l h d)"), k_out).then_inc(stored, 16)
                pool.dma_start(outs[3][0, bass.ds(l, 1), :, :, :].rearrange("l p h d -> p (l h d)"), vtok[:, 0, :]).then_inc(stored, 16)
                pool.dma_start(outs[4][0, bass.ds(l, 1), :, :].rearrange("l p d -> p (l d)"), ckvn[:, 0, :]).then_inc(stored, 16)
                pool.dma_start(outs[5][0, bass.ds(l, 1), :, :].rearrange("l p d -> p (l d)"), kr[:, 0, HD:QKD]).then_inc(stored, 16)
                pool.wait_ge(stored, 16 * OUT_DMAS * l + 16 * OUT_DMAS)
                pool.sem_inc(out_free, 1)

        def copy_out(eng, l, parity, lo, hi, dst, width=512, parts=P, scale=None, after=None):
            for j in range(lo, hi):
                if j % 2 != parity:
                    continue
                i = j - lo
                eng.wait_ge(item_ps, ITEMS * l + j + 1)
                w = width(i) if callable(width) else width
                out = dst(i)
                src = bank[j % 4][0:parts, 0:w]
                if len(out.shape) == 3:
                    src = src.rearrange("p (a b) -> p a b", a=out.shape[1])
                if parity == 0:
                    if scale is None:
                        ins = nc.scalar.activation(out, src, ACT.Copy)
                    else:
                        ins = nc.scalar.activation(out, src, ACT.Copy, scale=scale(i))
                    ins.then_inc(item_act, 1)
                else:
                    if scale is None:
                        ins = nc.vector.tensor_copy(out, src)
                    else:
                        ins = nc.vector.tensor_scalar(out, src, scale(i), None, ALU.mult)
                    ins.then_inc(item_dve, 1)

        def copies_projection(eng, l, parity):
            copy_out(eng, l, parity, IT_V, IT_QK, lambda i: vtok[:, i, :])
            copy_out(eng, l, parity, IT_QK, IT_KOUT, lambda i: qkT[:, i, :], width=TOK)

        def copies_latent(eng, l, parity):
            copy_out(eng, l, parity, IT_KOUT, IT_KC, lambda i: k_out)
            copy_out(eng, l, parity, IT_KC, IT_CQT, lambda i: kcT.rearrange("p a b -> p (a b)"))
            copy_out(eng, l, parity, IT_CQT, IT_CKVT, lambda i: cqT[:, i, :], width=TOK,
                     scale=lambda i: vec[:, bass.ds(l, 1), 64 + i:65 + i].rearrange("p a b -> p (a b)"))
            copy_out(eng, l, parity, IT_CKVT, IT_KRT, lambda i: ckvT)
            copy_out(eng, l, parity, IT_KRT, IT_QM, lambda i: krT[0:QKD, :], parts=QKD)
            copy_out(eng, l, parity, IT_QM, IT_VM, lambda i: qtok[:, i // 2, 512 * (i % 2):512 + 256 * (i % 2)],
                     width=lambda i: 512 - 256 * (i % 2))

        def copies_values(eng, l, parity):
            copy_out(eng, l, parity, IT_VM, IT_KM, lambda i: vm[:, i, :])
            copy_out(eng, l, parity, IT_KM, IT_QMT, lambda i: kmT[0:HD, i, :], parts=HD)

        def copies_q(eng, l, parity):
            copy_out(eng, l, parity, IT_QMT, IT_OT, lambda i: qmT[0:QKD, i, :], width=TOK, parts=QKD)

        def copies_o(eng, l, parity):
            copy_out(eng, l, parity, IT_OT, IT_HTOK, lambda i: hT[:, i, :], width=TOK)

        def copies_htok(eng, l, parity):
            copy_out(eng, l, parity, IT_HTOK, ITEMS, lambda i: htok[:, i // 2, 512 * (i % 2):512 * (i % 2) + 512])

        def unit(u):
            kind, r = divmod(u, 12)
            pair, t = divmod(r, 3)
            return kind, pair, t, (P if t == 0 else TOK)

        @block.tensor
        def _(pe):
            pe.sem_inc(selT_ps, 1)
            pe.wait_ge(consts_in, 16)
            pe.wait_ge(x_in, 32)
            for k in range(KD):
                if k >= 2:
                    pe.wait_ge(x_evac, k - 1)
                for t in range(NT):
                    ins = nc.tensor.transpose(bank[k % 2][:, P * t:P * t + P], tokx[:, t, P * k:P * k + P], ident)
                ins.then_inc(x_ps, 1)
            pe.wait_ge(rows_in, 16 * 11)
            for i in range(3):
                ins = nc.tensor.transpose(bank[2][:, P * i:P * i + 66], rows[0:66, P * i:P * i + P], ident[0:66, 0:66])
            ins.then_inc(vec_ps, 1)
            pe.wait_ge(cond_ready, 1)

            def loaded(l, n):
                pe.wait_ge(slot_full[n % NSLOT], 16 * (LAYER_SLOTS // NSLOT * l + n // NSLOT + 1))

            def release(l, items):
                pe.wait_ge(item_ps, ITEMS * l + items)
                pe.sem_inc(slot_free, 1)

            def norm(l, i):
                for k in range(KD):
                    pe.wait_ge(sq_ready, 2 * KD * l + KD * i + k + 1)
                    ins = nc.tensor.matmul(bank[4][:, 0:TOK], ones, hT[:, k, :], start=(k == 0), stop=(k == KD - 1))
                ins.then_inc(ss_ps, 1)

            def ada_piece(l, j, n):
                loaded(l, n)
                w = tiles(slot(n), KD)
                for m in range(4):
                    c = 2 * (4 * j + m)
                    for k in range(KD):
                        ins = nc.tensor.matmul(bank[7][:, c:c + 2], w[:, k, P * m:P * m + P], cond[:, k, :],
                                               start=(k == 0), stop=(k == KD - 1))
                ins.then_inc(slot_free, 1)

            def expert_pass(l, q, c0):
                def slot_ready(i):
                    pe.wait_ge(slot_full[i % NSLOT], 16 * (i // NSLOT + 1) + 16 * c0)

                pe.wait_ge(sel_ready, q + 1)
                pe.wait_ge(scat_done, 8 * q + 8)
                for half in range(2):
                    for d in range(4):
                        k = 4 * half + d
                        for t in range(NT):
                            ins = nc.tensor.matmul(bank[6 + half][:, P * d:P * d + P], htok[:, t, P * k:P * k + P],
                                                   sel_m[:, t, :], start=(t == 0), stop=(t == NT - 1))
                    ins.then_inc(gather_ps, 1)
                pe.wait_ge(hg_act, q + 1)
                for t in range(NT):
                    nc.tensor.transpose(bank[6][:, P * t:P * t + P], sel_m[:, t, :], ident)
                for t in range(NT):
                    ins = nc.tensor.matmul(bank[6][:, TOK:TOK + 4], sel_m[:, t, :], gates4[:, t, :],
                                           start=(t == 0), stop=(t == NT - 1))
                ins.then_inc(selT_ps, 1)
                pe.wait_ge(hg_dve, q + 1)

                def gate_up(e, i):
                    for which in range(2):
                        slot_ready(i + which)
                        if which == 0:
                            pe.wait_ge(hid_ready, 4 * q + e + 2)
                        w = tiles(slot(i + which), KD)
                        for k in range(KD):
                            ins = nc.tensor.matmul(bank[2 + 2 * which + e % 2][:, :], hg[:, k, :], w[:, k, :],
                                                   start=(k == 0), stop=(k == KD - 1))
                        ins.then_inc(slot_free, 1)

                def down(e, i):
                    pe.wait_ge(hid_ready, 4 * q + e + 4)
                    b = 6 + (e + 1) % 2
                    if e == 0:
                        pass
                    elif e == 1:
                        pe.wait_ge(selT_ready, q + 1)
                    else:
                        pe.wait_ge(hidT_ready, 4 * q + e - 1)
                    for c in range(4):
                        ins = nc.tensor.transpose(bank[b][:, P * c:P * c + P], hid[e % 2][:, P * c:P * c + P], ident)
                    ins.then_inc(hidT_ps, 1)
                    slot_ready(i)
                    pe.wait_ge(hidT_ready, 4 * q + e + 1)
                    w = tiles(slot(i), 4)
                    for half in range(2):
                        for c in range(4):
                            ins = nc.tensor.matmul(bank[half][:, :], hidT[e % 2][:, c, :], w[:, c, 512 * half:512 * half + 512],
                                                   start=(e == 0 and c == 0), stop=(e == 3 and c == 3))
                    ins.then_inc(slot_free, 1)

                gate_up(0, 0)
                gate_up(1, 2)
                down(0, 4)
                gate_up(2, 5)
                down(1, 7)
                gate_up(3, 8)
                down(2, 10)
                down(3, 11)
                pe.wait_ge(y_act, q + 1)
                pe.wait_ge(y_dve, q + 1)
                for k in range(KD):
                    if k < 2:
                        pe.wait_ge(hidT_ready, 4 * q + 4)
                    else:
                        pe.wait_ge(scat_done, 8 * q + 8 + k - 1)
                    nc.tensor.matmul(bank[6 + k % 2][:, 0:TOK], y_sb[:, P * k:P * k + P], selT[:, 0:TOK],
                                     start=True, stop=True).then_inc(scat_ps, 1)

            with pe.Fori(0, DEPTH) as l:
                norm(l, 0)
                for j in range(ADA_EARLY):
                    ada_piece(l, j, j)
                loaded(l, W_REST)
                w = tiles(slot(W_REST)[:, 0:KD * REST], KD)
                for t in range(NT):
                    item_free(pe, l, IT_REST + t)
                    for k in range(KD):
                        if t == 0:
                            pe.wait_ge(h_ready, 2 * KD * l + k + 1)
                        ins = nc.tensor.matmul(bank[(IT_REST + t) % 4][:, 0:REST], hT[:, k, P * t:P * t + P], w[:, k, :],
                                               start=(k == 0), stop=(k == KD - 1))
                    ins.then_inc(item_ps, 1)
                release(l, IT_V)
                loaded(l, W_V)
                w = tiles(slot(W_V), KD)
                for t in range(NT):
                    item_free(pe, l, IT_V + t)
                    for k in range(KD):
                        ins = nc.tensor.matmul(bank[(IT_V + t) % 4][:, :], hT[:, k, P * t:P * t + P], w[:, k, :],
                                               start=(k == 0), stop=(k == KD - 1))
                    ins.then_inc(item_ps, 1)
                release(l, IT_QK)
                for half in range(2):
                    loaded(l, W_Q + half)
                    w = tiles(slot(W_Q + half), KD)
                    for m in range(4):
                        j = IT_QK + 4 * half + m
                        item_free(pe, l, j)
                        for k in range(KD):
                            ins = nc.tensor.matmul(bank[j % 4][:, 0:TOK], w[:, k, P * m:P * m + P], hT[:, k, :],
                                                   start=(k == 0), stop=(k == KD - 1))
                        ins.then_inc(item_ps, 1)
                    release(l, IT_QK + 4 * half + 4)
                item_free(pe, l, IT_KOUT)
                item_wait(pe, l, IT_KOUT - 1)
                item_wait(pe, l, IT_KOUT - 2)
                for m in range(4):
                    ins = nc.tensor.transpose(bank[IT_KOUT % 4][:, P * m:P * m + P], qkT[:, 4 + m, 0:P], ident)
                ins.then_inc(item_ps, 1)
                item_free(pe, l, IT_KC)
                pe.wait_ge(cache_in, 64 * l + 64)
                for m in range(4):
                    ins = nc.tensor.transpose(bank[IT_KC % 4][:, P * m:P * m + P], kc_tok[:, P * m:P * m + P], ident)
                ins.then_inc(item_ps, 1)
                pe.wait_ge(lora_norm, l + 1)
                for i in range(2):
                    item_free(pe, l, IT_CQT + i)
                    for t in range(NT):
                        ins = nc.tensor.transpose(bank[(IT_CQT + i) % 4][:, P * t:P * t + P], cqn[:, t, P * i:P * i + P], ident)
                    ins.then_inc(item_ps, 1)
                item_free(pe, l, IT_CKVT)
                for m in range(4):
                    ins = nc.tensor.transpose(bank[IT_CKVT % 4][:, P * m:P * m + P], ckvn[:, m, :], ident)
                ins.then_inc(item_ps, 1)
                pe.wait_ge(kr_ready, l + 1)
                item_free(pe, l, IT_KRT)
                for m in range(4):
                    ins = nc.tensor.transpose(bank[IT_KRT % 4][0:QKD, P * m:P * m + P], kr[:, m, :], ident)
                ins.then_inc(item_ps, 1)
                item_wait(pe, l, IT_CQT)
                item_wait(pe, l, IT_CQT + 1)
                loaded(l, W_UQ)
                w = tiles(slot(W_UQ)[:, 0:2 * HEADS * QKD], 2)
                for t in range(NT):
                    for half in range(2):
                        j = IT_QM + 2 * t + half
                        n = 512 - 256 * half
                        item_free(pe, l, j)
                        for k in range(2):
                            ins = nc.tensor.matmul(bank[j % 4][:, 0:n], cqT[:, k, P * t:P * t + P], w[:, k, 512 * half:512 * half + n],
                                                   start=(k == 0), stop=(k == 1))
                        ins.then_inc(item_ps, 1)
                release(l, IT_VM)
                item_wait(pe, l, IT_CKVT)
                loaded(l, W_UKV)
                wkv = slot(W_UKV)[:, 0:D].rearrange("p (h two d) -> p h two d", h=HEADS, two=2)
                for m in range(4):
                    item_free(pe, l, IT_VM + m)
                    nc.tensor.matmul(bank[(IT_VM + m) % 4][:, :].rearrange("p (h d) -> p h d", h=HEADS), ckvT[:, P * m:P * m + P],
                                     wkv[:, :, 1, :], start=True, stop=True).then_inc(item_ps, 1)
                for h in range(HEADS):
                    item_free(pe, l, IT_KM + h)
                    ins = nc.tensor.matmul(bank[(IT_KM + h) % 4][0:HD, :], wkv[:, h, 0, :], ckvT[:, :], start=True, stop=True)
                    ins.then_inc(item_ps, 1)
                release(l, IT_QMT)
                pe.wait_ge(q_roped, l + 1)
                for h in range(HEADS):
                    item_free(pe, l, IT_QMT + h)
                    for t in range(NT):
                        ins = nc.tensor.transpose(bank[(IT_QMT + h) % 4][0:QKD, P * t:P * t + P], qtok[:, t, QKD * h:QKD * h + QKD], ident)
                    ins.then_inc(item_ps, 1)
                for j in range(IT_OT - 4, IT_OT):
                    item_wait(pe, l, j)
                pe.wait_ge(kr_spread, l + 1)

                def scores(u):
                    kind, pair, t, n = unit(u)
                    if u >= 2:
                        pe.wait_ge(exp_ready, UNITS * l + u - 1)
                    for i in range(2):
                        b = bank[2 * (u % 2) + i]
                        if kind == 0:
                            r = slice(HD * i, HD * i + HD)
                            q = qkT[r, pair, P * t:P * t + P]
                            if t == 0:
                                ins = nc.tensor.matmul(b[:, 0:P], q, qkT[r, 4 + pair, 0:P], start=True, stop=True)
                            else:
                                nc.tensor.matmul(b[:, 0:P], q, kcT[r, pair, :], start=True, stop=True)
                                ins = nc.tensor.matmul(b[:, P:TOK], q, qkT[r, 4 + pair, P:TOK], start=True, stop=True)
                        else:
                            h = 2 * pair + i
                            ins = nc.tensor.matmul(b[:, 0:n], qmT[0:QKD, h, P * t:P * t + P],
                                                   kmT[0:QKD, h, 0:P] if t == 0 else kmT[0:QKD, h, P:4 * P], start=True, stop=True)
                    ins.then_inc(score_ps, 1)

                scores(0)
                scores(1)
                for u in range(UNITS + 1):
                    if u < UNITS:
                        n = unit(u)[3]
                        pe.wait_ge(exp_ready, UNITS * l + u + 1)
                        for i in range(2):
                            if u >= 1:
                                pe.wait_ge(probT_act if i == 0 else probT_dve, UNITS * l + u)
                            for c in range(n // P):
                                ins = nc.tensor.transpose(bank[4 + i][:, P * c:P * c + P], prob[:, u % 2, i, P * c:P * c + P], ident)
                            ins.then_inc(probT_ps, 1)
                    if u + 2 < UNITS:
                        scores(u + 2)
                    if u >= 1:
                        w = u - 1
                        kind, pair, t, n = unit(w)
                        if w >= 1:
                            pe.wait_ge(o_ready, UNITS * l + w + 1)
                        for i in range(2):
                            pe.wait_ge(probT_act if i == 0 else probT_dve, UNITS * l + w + 1)
                            h = 2 * pair + i
                            for c in range(n // P):
                                if kind == 0:
                                    v = vtok[:, 0, HD * h:HD * h + HD] if t == 0 else (
                                        vc[:, HD * h:HD * h + HD] if c == 0 else vtok[:, c, HD * h:HD * h + HD])
                                else:
                                    v = vm[:, 0 if t == 0 else 1 + c, HD * h:HD * h + HD]
                                ins = nc.tensor.matmul(bank[6][:, HD * i:HD * i + HD], probT[:, w % 2, i, P * c:P * c + P], v,
                                                       start=(c == 0), stop=(c == n // P - 1))
                        ins.then_inc(o_ps, 1)
                    if u % 3 == 2:
                        j = u // 3
                        if j == 0:
                            pe.wait_ge(mod_ready, 2 * l + 1)
                        ada_piece(l, ADA_EARLY + j, ADA_LATE + j)
                pe.wait_ge(o_ready, UNITS * l + UNITS + 1)
                for k in range(KD):
                    item_free(pe, l, IT_OT + k)
                    for t in range(NT):
                        ins = nc.tensor.transpose(bank[(IT_OT + k) % 4][:, P * t:P * t + P], otok[:, t, P * k:P * k + P], ident)
                    ins.then_inc(item_ps, 1)
                for half in range(2):
                    loaded(l, W_OUT + half)
                    w = tiles(slot(W_OUT + half), KD)
                    for m in range(4):
                        c = 4 * half + m
                        if c >= 2:
                            pe.wait_ge(x_updated, 8 * l + c - 1)
                        for k in range(KD):
                            if c == 0:
                                item_wait(pe, l, IT_OT + k)
                            ins = nc.tensor.matmul(bank[4 + c % 2][:, 0:TOK], w[:, k, P * m:P * m + P], hT[:, k, :],
                                                   start=(k == 0), stop=(k == KD - 1))
                        ins.then_inc(wo_ps, 1)
                    pe.wait_ge(wo_ps, 8 * l + 4 * half + 4)
                    pe.sem_inc(slot_free, 1)
                pe.wait_ge(x_updated, 8 * l + 8)
                norm(l, 1)
                for t in range(NT):
                    for k in range(KD):
                        if t == 0:
                            pe.wait_ge(h_ready, 2 * KD * l + KD + k + 1)
                        ins = nc.tensor.matmul(bank[5][:, E_ALL * t:E_ALL * t + E_ALL], hT[:, k, P * t:P * t + P], w_r[:, k, :],
                                               start=(k == 0), stop=(k == KD - 1))
                ins.then_inc(logit_ps, 1)
                for t in range(NT):
                    for half in range(2):
                        j = IT_HTOK + 2 * t + half
                        item_free(pe, l, j)
                        for c in range(4):
                            ins = nc.tensor.transpose(bank[j % 4][:, P * c:P * c + P], hT[:, 4 * half + c, P * t:P * t + P], ident)
                        ins.then_inc(item_ps, 1)
                pe.wait_ge(hot_ready, l + 1)
                for t in range(NT + 1):
                    for s in range(min(t, NT - 1) + 1):
                        ins = nc.tensor.matmul(bank[5][:, 64 + 4 * t:68 + 4 * t], tri if s == t else ones, one_hot[:, s, :],
                                               start=(s == 0), stop=(s == min(t, NT - 1)))
                ins.then_inc(rank_ps, 1)
                for j in range(ITEMS - 4, ITEMS):
                    item_wait(pe, l, j)
                passed(pe)
                with pe.Fori(0, GROUPS) as p:
                    expert_pass(l, l * PASSES + p, l * (LAYER_SLOTS // NSLOT) + p * 3 + W_MOE // NSLOT)
                pe.wait_ge(routed, l + 1)
                passed(pe)
                for o in range(2):
                    p = GROUPS + o
                    q = l * PASSES + p
                    owned = [(gather_ps, 2 * q, 2), (selT_ps, q + 1, 1), 
                             (hidT_ps, 4 * q, 4), (scat_ps, 8 * q, 8),
                             (slot_free, NSLOT + LAYER_SLOTS * l + W_MOE + 12 * p, 12)]
                    overflow(pe, l, o, owned, lambda: expert_pass(
                        l, q, l * (LAYER_SLOTS // NSLOT) + p * 3 + W_MOE // NSLOT))
            norm(DEPTH, 0)
            for t in range(NT):
                for half in range(2):
                    i = 2 * t + half
                    if i >= 2:
                        pe.wait_ge(x_evac, KD + i - 1)
                    for c in range(4):
                        k = 4 * half + c
                        if t == 0:
                            pe.wait_ge(h_ready, 2 * KD * DEPTH + k + 1)
                        ins = nc.tensor.transpose(bank[i % 2][:, P * c:P * c + P], hT[:, k, P * t:P * t + P], ident)
                    ins.then_inc(y_ps, 1)

        @block.scalar
        def _(act):
            act.wait_ge(vec_ready, 1)
            nc.scalar.activation(cond_e, vec[:, 2, 0:16], ACT.Exp, scale=-1.0).then_inc(cond_exp, 1)
            act.wait_ge(eps_ready, 1)
            act.wait_ge(x_evac, KD)

            def norm(l, i):
                n = 2 * l + i
                for k in range(KD):
                    nc.scalar.activation(hT[:, k, :], xT[:, k, :], ACT.Square).then_inc(sq_ready, 1)
                act.wait_ge(ss_ps, n + 1)
                nc.scalar.activation(rstd, bank[4][:, 0:TOK], ACT.Sqrt, bias=eps, scale=1.0 / D).then_inc(std_ready, 1)

            def modulate(l, i):
                act.wait_ge(mod_ready, 2 * l + 1 + i)
                for k in range(KD):
                    act.wait_ge(xn_ready, 2 * KD * l + KD * i + k + 1)
                    for lo, hi, s in SEGS:
                        ins = nc.scalar.activation(hT[:, k, lo:hi], xn[:, k, lo:hi], ACT.Identity,
                                                   bias=mod[:, 3 * i, k, s:s + 1], scale=gain[:, i, k, s:s + 1])
                    ins.then_inc(h_ready, 1)

            def expert_pass(q, c0):
                act.wait_ge(gather_ps, 2 * q + 1)
                nc.scalar.activation(hg[:, 0:4, :], bank[6].rearrange("p (k n) -> p k n", k=4), ACT.Copy).then_inc(hg_act, 1)

                def hidden_T(e):
                    act.wait_ge(hidT_ps, 4 * q + e + 1)
                    nc.scalar.activation(hidT[e % 2], bank[6 + (e + 1) % 2].rearrange("p (k n) -> p k n", k=4),
                                         ACT.Copy).then_inc(hidT_ready, 1)

                for e in range(E_GROUP):
                    act.wait_ge(slot_free, c0 + (1, 3, 6, 9)[e])
                    act.wait_ge(hid_ready, 4 * q + e + 3)
                    nc.scalar.activation(th, bank[2 + e % 2], ACT.Tanh, scale=0.5).then_inc(tanh_ready, 1)
                    if e >= 1:
                        hidden_T(e - 1)
                hidden_T(E_GROUP - 1)
                act.wait_ge(slot_free, c0 + 12)
                nc.scalar.activation(y_sb[:, 0:512], bank[0], ACT.Copy).then_inc(y_act, 1)

            with act.Fori(0, DEPTH) as l:
                st = Steps(act, act_step, STEPS * l)
                act.wait_ge(out_free, l + 1)
                act.wait_ge(scat_done, 8 * PASSES * l + 8)
                norm(l, 0)
                modulate(l, 0)
                copy_out(act, l, 0, IT_REST, IT_V, lambda i: rest[:, i, :], width=REST)
                copy_out(act, l, 0, IT_V, IT_QK, lambda i: vtok[:, i, :])
                for t in range(NT):
                    item_wait(act, l, IT_REST + t)
                    nc.scalar.activation(cqn[:, t, :], rest[:, t, 0:RANK_Q], ACT.Square, accum_out=stat[:, t:t + 1])
                    ckt = 0 if t == 0 else t + 1
                    st.did(nc.scalar.activation(ckvn[:, ckt, :], rest[:, t, RANK_Q:RANK_Q + RANK_KV], ACT.Square,
                                                accum_out=stat[:, 3 + t:4 + t]))
                st.sync()
                nc.scalar.activation(rstat[:, 0:3], stat[:, 0:3], ACT.Sqrt, bias=eps, scale=1.0 / RANK_Q)
                nc.scalar.activation(rstat[:, 3:6], stat[:, 3:6], ACT.Sqrt, bias=eps, scale=1.0 / RANK_KV).then_inc(lora_stat, 1)
                copy_out(act, l, 0, IT_QK, IT_KOUT, lambda i: qkT[:, i, :], width=TOK)
                copies_latent(act, l, 0)
                copies_values(act, l, 0)
                copies_q(act, l, 0)

                def exps(u):
                    kind, pair, t, n = unit(u)
                    act.wait_ge(max_ready, UNITS * l + u + 1)
                    if u >= 2:
                        act.wait_ge(probT_ps, 2 * UNITS * l + 2 * (u - 1))
                    for i in range(2):
                        c = 2 * (u % 2) + i
                        ins = nc.scalar.activation(prob[:, u % 2, i, 0:n], bank[c][:, 0:n], ACT.Exp,
                                                   bias=neg_max[:, 4 + c:5 + c], scale=(NA_SCALE, MLA_SCALE)[kind],
                                                   accum_out=sums[:, 2 * (u % 4) + i:2 * (u % 4) + i + 1])
                    ins.then_inc(exp_ready, 1)

                exps(0)
                for u in range(UNITS):
                    n = unit(u)[3]
                    if u + 1 < UNITS:
                        exps(u + 1)
                    act.wait_ge(probT_ps, 2 * UNITS * l + 2 * u + 1)
                    if u >= 2:
                        act.wait_ge(o_ps, UNITS * l + u - 1)
                    nc.scalar.activation(probT[:, u % 2, 0, 0:n], bank[4][:, 0:n], ACT.Copy).then_inc(probT_act, 1)
                copies_o(act, l, 0)
                act.wait_ge(x_updated, 8 * l + 8)
                norm(l, 1)
                modulate(l, 1)
                act.wait_ge(logit_ps, l + 1)
                nc.scalar.activation(rt[:, 0, :], bank[5][:, 0:48], ACT.Exp, scale=-1.0).then_inc(logit_exp, 1)
                copies_htok(act, l, 0)
                with act.Fori(0, GROUPS) as p:
                    expert_pass(l * PASSES + p, pass_used(l, p))
                act.wait_ge(routed, l + 1)
                passed(act)
                for o in range(2):
                    q = l * PASSES + GROUPS + o
                    owned = [(hg_act, q, 1), (tanh_ready, 4 * q, 4), (hidT_ready, 4 * q, 4), (y_act, q, 1)]
                    overflow(act, l, o, owned, lambda: expert_pass(q, pass_used(l, GROUPS + o)))
                st.close(STEPS)
            act.wait_ge(scat_done, 8 * PASSES * DEPTH + 8)
            norm(DEPTH, 0)
            for i in range(0, 2 * NT, 2):
                act.wait_ge(y_ps, i + 1)
                if i == 0:
                    act.wait_ge(h_ready, 2 * KD * DEPTH + KD)
                if i >= 1:
                    act.wait_ge(x_evac, KD + i)
                nc.scalar.activation(tokx[:, i // 2, 0:512], bank[0], ACT.Copy).then_inc(x_evac, 1)

        @block.vector
        def _(dve):
            v = nc.vector
            v.memset(eps, EPS).then_inc(eps_ready, 1)
            for k in range(KD):
                dve.wait_ge(x_ps, k + 1)
                v.tensor_copy(xT[:, k, :], bank[k % 2][:, 0:TOK]).then_inc(x_evac, 1)
            dve.wait_ge(vec_ps, 1)
            v.tensor_copy(vec, bank[2][:, 0:3 * P].rearrange("p (a b) -> p a b", a=3)[:, :, 0:66]).then_inc(vec_ready, 1)
            st = Steps(dve, dve_step, 0)
            dve.wait_ge(cond_exp, 1)
            st.did(v.tensor_scalar(cond_e, cond_e, 1.0, None, ALU.add))
            st.sync()
            st.did(v.reciprocal(cond_e, cond_e))
            st.sync()
            v.tensor_tensor(cond.rearrange("p k s -> p s k"), vec[:, 2, 0:16].rearrange("p (s k) -> p s k", s=2),
                            cond_e.rearrange("p (s k) -> p s k", s=2), ALU.mult).then_inc(cond_ready, 1)
            st.close(STEPS)
            dve.sem_inc(hid_ready, 3)
            dve.sem_inc(scat_done, 8)

            def norm(l, i, final=False):
                n = 2 * l + i
                dve.wait_ge(std_ready, n + 1)
                st.did(v.reciprocal(rstd, rstd))
                st.sync()
                for k in range(KD):
                    if final:
                        v.scalar_tensor_tensor(hT[:, k, :], xT[:, k, :], vec[:, 2, 16 + k:17 + k], rstd, ALU.mult,
                                               ALU.mult).then_inc(h_ready, 1)
                    else:
                        v.tensor_tensor(xn[:, k, :], xT[:, k, :], rstd, ALU.mult).then_inc(xn_ready, 1)

            def rope(x, t, heads):
                c = cos[:, t - 1, :].unsqueeze(1).to_broadcast([P, heads, ROPE])
                s = sin[:, t - 1, :].rearrange("p (a b f) -> p a b f", a=2, b=2)
                swapped = rope_t[:, 0:heads * ROPE].rearrange("p (h a b f) -> p h a b f", h=heads, a=2, b=2)
                xv = x.rearrange("p h (a b f) -> p h a b f", a=2, b=2)
                for b in range(2):
                    for ax in range(2):
                        st.did(v.tensor_tensor(swapped[:, :, ax, b, :], xv[:, :, ax, 1 - b, :],
                                               s[:, ax, b, :].unsqueeze(1).to_broadcast([P, heads, 8]), ALU.mult))
                st.sync()
                st.did(v.tensor_tensor(x, x, c, ALU.mult))
                st.sync()
                st.did(v.tensor_tensor(x, x, rope_t[:, 0:heads * ROPE].rearrange("p (h f) -> p h f", h=heads), ALU.add))

            def ranks(s, n, width, out):
                cv = cmp[:, 0:4 * n * width].rearrange("p (j g e) -> p j g e", j=width, g=n)
                for j in range(width):
                    if j:
                        st.did(v.tensor_tensor(cv[:, j, :, 0:j], s[:, :, j:j + 1].to_broadcast([P, n, j]), s[:, :, 0:j], ALU.is_gt))
                    st.did(v.tensor_tensor(cv[:, j, :, j:width], s[:, :, j:j + 1].to_broadcast([P, n, width - j]), s[:, :, j:width], ALU.is_ge))
                st.sync()
                st.did(v.tensor_reduce(out, cmp[:, 0:width * n * width].rearrange("p (j r) -> p r j", j=width), AX.X, ALU.add))
                st.sync()

            def route(l):
                dve.wait_ge(logit_exp, l + 1)
                aff, sel, rank, chosen, tmp = (rt[:, i, :] for i in range(1, 6))
                gs, grank = rt[:, 6, 0:12], rt[:, 6, 12:24]
                den = rt[:, 6, 24:27]
                e1 = rt[:, 0, :]

                def do(ins):
                    st.did(ins)
                    st.sync()

                def rows4(x):
                    return x.rearrange("p (g e) -> p g e", e=4)

                do(v.tensor_scalar(e1, e1, 1.0, None, ALU.add))
                do(v.reciprocal(aff, e1))
                do(v.tensor_tensor(tiles(sel, NT), tiles(aff, NT), b_r.unsqueeze(1).to_broadcast([P, NT, E_ALL]), ALU.add))
                ranks(rows4(sel), 12, 4, rank)
                do(v.tensor_scalar(chosen, rank, 2.5, None, ALU.is_lt))
                do(v.tensor_tensor(tmp, sel, chosen, ALU.mult))
                do(v.tensor_reduce(gs, rows4(tmp), AX.X, ALU.add))
                ranks(rows4(gs), NT, 4, grank)
                v.tensor_scalar(one_hot, rows4(grank), 1.5, None, ALU.is_lt).then_inc(hot_ready, 1)
                dve.wait_ge(hot_ready, l + 1)
                do(v.tensor_tensor(rows4(chosen), rows4(chosen),
                                   one_hot.rearrange("p t g -> p (t g)").unsqueeze(2).to_broadcast([P, 12, 4]), ALU.mult))
                do(v.tensor_tensor(tmp, aff, chosen, ALU.mult))
                do(v.tensor_reduce(den, tiles(tmp, NT), AX.X, ALU.add))
                do(v.reciprocal(den, den))
                do(v.scalar_tensor_tensor(tiles(tmp, NT), tiles(tmp, NT), 0.5, den.unsqueeze(2).to_broadcast([P, NT, E_ALL]),
                                          ALU.mult, ALU.mult))
                do(v.tensor_reduce(gates4, tmp.rearrange("p (t g e) -> p t e g", t=NT, g=GROUPS), AX.X, ALU.add))
                copies_htok(dve, l, 1)
                dve.wait_ge(rank_ps, l + 1)
                count = small[:, 0, 0:4]
                do(v.tensor_scalar(rk1, bank[5][:, 64:76].rearrange("p (t g) -> p t g", t=NT), 1.0, None, ALU.add))
                do(v.tensor_copy(count, bank[5][:, 76:80]))
                do(v.tensor_tensor(prod, rk1, one_hot, ALU.mult))
                do(v.tensor_scalar(slot_of[:, :, 0:4], prod, -1.0, None, ALU.add))
                flag = small[:, 1, 0:8]
                do(v.tensor_scalar(flag[:, 0:4], count, 128.5, None, ALU.is_gt))
                do(v.tensor_scalar(flag[:, 4:8], count, 256.5, None, ALU.is_gt))
                before = small[:, 2, 0:8]
                do(v.memset(before[:, 0:1], 0.0))
                for i in range(1, 8):
                    do(v.tensor_tensor(before[:, i:i + 1], before[:, i - 1:i], flag[:, i - 1:i], ALU.add))
                for o in range(2):
                    mine, t8, act_g, base = small[:, 3, 0:8], small[:, 4, 0:8], small[:, 5, 0:4], small[:, 6, 0:4]
                    do(v.tensor_scalar(mine, before, float(o), None, ALU.is_equal))
                    do(v.tensor_tensor(mine, mine, flag, ALU.mult))
                    do(v.tensor_reduce(ctl_f[:, o:o + 1], mine, AX.X, ALU.add))
                    do(v.tensor_tensor(t8, mine, gidx.rearrange("p a b -> p (a b)"), ALU.mult))
                    do(v.tensor_reduce(ctl_f[:, 2 + o:3 + o], t8, AX.X, ALU.add))
                    do(v.tensor_tensor(act_g, mine[:, 0:4], mine[:, 4:8], ALU.add))
                    do(v.tensor_tensor(base, act_g, mine[:, 4:8], ALU.add))
                    do(v.tensor_scalar(base, base, 128.0, None, ALU.mult))
                    do(v.tensor_tensor(prod, rk1, base.unsqueeze(1).to_broadcast([P, NT, 4]), ALU.subtract))
                    do(v.tensor_tensor(prod, prod, one_hot, ALU.mult))
                    do(v.tensor_tensor(prod, prod, act_g.unsqueeze(1).to_broadcast([P, NT, 4]), ALU.mult))
                    do(v.tensor_reduce(slot_of[:, :, 4 + o], prod, AX.X, ALU.add))
                do(v.tensor_scalar(slot_of[:, :, 4:6], slot_of[:, :, 4:6], -1.0, None, ALU.add))
                v.tensor_copy(ctl[:, :], ctl_f).then_inc(routed, 1)

            def expert_pass(q, c0, col):
                ms = Steps(dve, dve_mstep, MSTEPS * q)
                dve.wait_ge(selT_ps, q + 1)
                for t in range(NT):
                    ins = v.tensor_scalar(sel_m[:, t, :], iota, col(t), None, ALU.is_equal)
                ins.then_inc(sel_ready, 1)
                dve.wait_ge(gather_ps, 2 * q + 2)
                v.tensor_copy(hg[:, 4:8, :], bank[7].rearrange("p (k n) -> p k n", k=4)).then_inc(hg_dve, 1)
                dve.wait_ge(selT_ps, q + 2)
                v.tensor_copy(selT, bank[6][:, 0:TOK + 4]).then_inc(selT_ready, 1)
                for e in range(E_GROUP):
                    dve.wait_ge(tanh_ready, 4 * q + e + 1)
                    ms.did(v.scalar_tensor_tensor(t1, th, 1.0, bank[2 + e % 2], ALU.add, ALU.mult))
                    ms.sync()
                    if e == 0:
                        dve.wait_ge(selT_ready, q + 1)
                    dve.wait_ge(slot_free, c0 + (2, 4, 7, 10)[e])
                    if e >= 2:
                        dve.wait_ge(hidT_ps, 4 * q + e - 1)
                    v.scalar_tensor_tensor(hid[e % 2], t1, selT[:, TOK + e:TOK + e + 1], bank[4 + e % 2], ALU.mult,
                                           ALU.mult).then_inc(hid_ready, 1)
                dve.wait_ge(slot_free, c0 + 12)
                v.tensor_copy(y_sb[:, 512:1024], bank[1]).then_inc(y_dve, 1)
                for k in range(KD):
                    dve.wait_ge(scat_ps, 8 * q + k + 1)
                    for lo, hi, s in SEGS:
                        ins = v.scalar_tensor_tensor(xT[:, k, lo:hi], bank[6 + k % 2][:, lo:hi], mod[:, 5, k, s:s + 1], xT[:, k, lo:hi],
                                                     ALU.mult, ALU.add)
                    ins.then_inc(scat_done, 1)
                ms.close(MSTEPS)

            def modulation(l, c0, c1):
                n = (c1 - c0) * KD
                b = vec[:, bass.ds(l, 1), KD * c0:KD * c1].rearrange("p a b -> p (a b)").unsqueeze(2).to_broadcast([P, n, 2])
                st.did(v.tensor_tensor(mod[:, c0:c1, :, :].rearrange("p c k s -> p (c k) s"),
                                       bank[7][:, 2 * KD * c0:2 * KD * c1].rearrange("p (m s) -> p m s", s=2), b, ALU.add))

            def gains(l, i):
                g = vec[:, bass.ds(l, 1), 48 + 8 * i:56 + 8 * i].rearrange("p a b -> p (a b)")
                st.sync()
                v.scalar_tensor_tensor(gain[:, i, :, :], mod[:, 1 + 3 * i, :, :], 1.0, g.unsqueeze(2).to_broadcast([P, KD, 2]),
                                       ALU.add, ALU.mult).then_inc(mod_ready, 1)

            with dve.Fori(0, DEPTH) as l:
                st = Steps(dve, dve_step, STEPS * l + STEPS)
                dve.wait_ge(out_free, l + 1)
                norm(l, 0)
                dve.wait_ge(slot_free, used(l, ADA_EARLY))
                modulation(l, 0, 2)
                gains(l, 0)
                copy_out(dve, l, 1, IT_REST, IT_V, lambda i: rest[:, i, :], width=REST)
                copy_out(dve, l, 1, IT_V, IT_QK, lambda i: vtok[:, i, :])
                copy_out(dve, l, 1, IT_QK, IT_KOUT, lambda i: qkT[:, i, :], width=TOK)
                dve.wait_ge(lora_stat, l + 1)
                st.did(v.reciprocal(rstat, rstat))
                st.sync()
                for t in range(NT):
                    kt = 0 if t == 0 else t + 1
                    st.did(v.tensor_copy(kr[:, kt, HD:QKD], rest[:, t, RANK_Q + RANK_KV:REST]))
                    st.did(v.tensor_scalar(cqn[:, t, :], rest[:, t, 0:RANK_Q], rstat[:, t:t + 1], None, ALU.mult))
                    st.did(v.scalar_tensor_tensor(ckvn[:, kt, :], rest[:, t, RANK_Q:RANK_Q + RANK_KV], rstat[:, 3 + t:4 + t],
                                                  kvg[:, bass.ds(l, 1), :].rearrange("p a b -> p (a b)"), ALU.mult, ALU.mult))
                st.sync()
                dve.sem_inc(lora_norm, 1)
                rope(kr[:, 2, HD:QKD].unsqueeze(1), 1, 1)
                st.sync()
                rope(kr[:, 3, HD:QKD].unsqueeze(1), 2, 1)
                st.sync()
                dve.sem_inc(kr_ready, 1)
                copies_latent(dve, l, 1)
                for t in range(1, NT):
                    item_wait(dve, l, IT_QM + 2 * t)
                    item_wait(dve, l, IT_QM + 2 * t + 1)
                    rope(qtok[:, t, :].rearrange("p (h e) -> p h e", h=HEADS)[:, :, HD:QKD], t, HEADS)
                    st.sync()
                dve.sem_inc(q_roped, 1)
                copies_values(dve, l, 1)
                copies_q(dve, l, 1)
                dve.wait_ge(bias_ready, l + 1)

                def maxes(u):
                    kind, pair, t, n = unit(u)
                    dve.wait_ge(score_ps, UNITS * l + u + 1)
                    c = 2 * (u % 2)
                    s2 = psum[:, c:c + 2, :]
                    if kind == 0 and t > 0:
                        at = GRID * (2 - 2 * (t - 1))
                        st.did(v.tensor_tensor(s2[:, :, P:TOK], s2[:, :, P:TOK], bias[:, 2 * pair:2 * pair + 2, at:at + LAT], ALU.add))
                        st.sync()
                    st.did(v.tensor_reduce(neg_max[:, c:c + 2], s2[:, :, 0:n], AX.X, ALU.max))
                    st.sync()
                    v.tensor_scalar(neg_max[:, 4 + c:6 + c], neg_max[:, c:c + 2], -(NA_SCALE, MLA_SCALE)[kind], None,
                                    ALU.mult).then_inc(max_ready, 1)

                maxes(0)
                maxes(1)
                for u in range(UNITS + 1):
                    if u < UNITS:
                        n = unit(u)[3]
                        dve.wait_ge(probT_ps, 2 * UNITS * l + 2 * u + 2)
                        if u >= 2:
                            dve.wait_ge(o_ps, UNITS * l + u - 1)
                        v.tensor_copy(probT[:, u % 2, 1, 0:n], bank[5][:, 0:n]).then_inc(probT_dve, 1)
                    if u + 2 < UNITS:
                        maxes(u + 2)
                    if u >= 1:
                        w = u - 1
                        kind, pair, t, n = unit(w)
                        c, cs = 2 * (w % 2), 2 * (w % 4)
                        st.did(v.reciprocal(rsum[:, c:c + 2], sums[:, cs:cs + 2]))
                        st.sync()
                        dve.wait_ge(o_ps, UNITS * l + w + 1)
                        v.tensor_tensor(otok[:, t, 512 * kind + P * pair:512 * kind + P * pair + P].rearrange("p (i d) -> p i d", i=2),
                                        bank[6][:, 0:P].rearrange("p (i d) -> p i d", i=2),
                                        rsum[:, c:c + 2].unsqueeze(2).to_broadcast([P, 2, HD]), ALU.mult).then_inc(o_ready, 1)
                dve.wait_ge(slot_free, used(l, ADA_LATE + 8))
                modulation(l, 2, 6)
                gains(l, 1)
                copies_o(dve, l, 1)
                dve.wait_ge(mod_ready, 2 * l + 2)
                for k in range(KD):
                    dve.wait_ge(wo_ps, 8 * l + k + 1)
                    for lo, hi, s in SEGS:
                        ins = v.scalar_tensor_tensor(xT[:, k, lo:hi], bank[4 + k % 2][:, lo:hi], mod[:, 2, k, s:s + 1], xT[:, k, lo:hi],
                                                     ALU.mult, ALU.add)
                    ins.then_inc(x_updated, 1)
                dve.wait_ge(x_updated, 8 * l + 8)
                norm(l, 1)
                route(l)
                with dve.Fori(0, GROUPS) as p:
                    expert_pass(l * PASSES + p, pass_used(l, p), lambda t: slot_of[:, t, bass.ds(p, 1)])
                dve.wait_ge(routed, l + 1)
                passed(dve)
                for o in range(2):
                    q = l * PASSES + GROUPS + o
                    owned = [(sel_ready, q, 1), (hg_dve, q, 1), (selT_ready, q, 1), (hid_ready, 4 * q + 3, 4),
                             (y_dve, q, 1), (scat_done, 8 * q + 8, 8), (dve_mstep, MSTEPS * q, MSTEPS)]
                    overflow(dve, l, o, owned, lambda: expert_pass(q, pass_used(l, GROUPS + o), lambda t: slot_of[:, t, GROUPS + o:GROUPS + o + 1]))
                dve.wait_ge(scat_done, 8 * PASSES * l + 8 * PASSES + 8)
                st.close(STEPS)
            st = Steps(dve, dve_step, STEPS * (DEPTH + 1))
            norm(DEPTH, 0, final=True)
            for i in range(1, 2 * NT, 2):
                dve.wait_ge(y_ps, i + 1)
                dve.wait_ge(x_evac, KD + i)
                v.tensor_copy(tokx[:, i // 2, 512:1024], bank[1]).then_inc(x_evac, 1)
                dve.wait_ge(x_evac, KD + i + 1)
                dve.sem_inc(y_ready, 1)


_INS = ["x_prompt", "x_sample", "cache_nat_k", "cache_nat_v", "cache_mla_ckv", "cache_mla_krope", "c", "c_ctx", "norm1_g",
        "norm2_g", "w_ada", "b_ada", "w_in", "q_norm_g", "w_uq", "kv_norm_g", "w_ukv", "rpb", "w_out", "w_router",
        "b_router", "w_gate", "w_up", "w_down", "final_norm_g"]
_OUTS = [(1, CTX, D), (1, LAT, D), (1, DEPTH, CTX, HEADS, HD), (1, DEPTH, CTX, HEADS, HD), (1, DEPTH, CTX, RANK_KV),
         (1, DEPTH, CTX, ROPE)]


def _constants():
    c = np.zeros((P, C_N), np.float32)
    c[:, C_ID:C_ID + P] = np.eye(P)
    c[:, C_TRI:C_TRI + P] = np.triu(np.ones((P, P)), 1)
    c[:, C_ONE:C_ONE + P] = 1.0
    c[:, C_IOTA:C_IOTA + P] = np.arange(P)
    q = np.arange(P) % GRID
    lo = np.clip(q - WIN_W // 2, 0, GRID - WIN_W)
    key = np.arange(GRID)
    inside = (key[None] >= lo[:, None]) & (key[None] < lo[:, None] + WIN_W)
    c[:, C_MASK:C_MASK + GRID] = np.where(inside, 0.0, -1e30)
    half = ROPE // 2
    freqs = (1.0 / (10000.0 ** (np.arange(0, half, 2, dtype=np.float32) / half))).astype(np.float32)
    for t in range(2):
        tok = np.arange(P) + P * t
        for ax, pos in enumerate((tok // GRID, tok % GRID)):
            ang = pos.astype(np.float32)[:, None] * freqs
            at = 32 * t + 16 * ax
            c[:, C_COS + at:C_COS + at + 16] = np.concatenate([np.cos(ang), np.cos(ang)], 1)
            c[:, C_SIN + at:C_SIN + at + 16] = np.concatenate([-np.sin(ang), np.sin(ang)], 1)
    c[:, C_GIDX:C_GIDX + 8] = np.arange(8) % 4
    return c


def kernel(**inputs):
    import concourse.bacc as bacc
    from concourse.bass_utils import run_bass_kernel_spmd as run

    nc = bacc.Bacc("TRN2", target_bir_lowering=False, num_devices=1)
    f32 = mybir.dt.float32
    arrays = {"in_" + n: np.ascontiguousarray(inputs[n]) for n in _INS}
    arrays["in_consts"] = _constants()
    args = {n: nc.dram_tensor("in_" + n, arrays["in_" + n].shape, f32, kind="ExternalInput").ap() for n in _INS + ["consts"]}
    outs = [nc.dram_tensor(f"out_{i}", shape, f32, kind="ExternalOutput").ap() for i, shape in enumerate(_OUTS)]
    skewed = nc.dram_tensor("bias_skewed", (DEPTH, HEADS, SKEW_HEAD), f32, kind="Internal")
    scratch = nc.dram_tensor("bias_padded", (DEPTH * HEADS, RPB_ROWS * GRID), f32, kind="Internal")
    build(nc, args, outs, scratch, skewed)
    r = run(nc, [arrays], core_ids=[0])
    return tuple(r.results[0][f"out_{i}"] for i in range(len(_OUTS)))
```
